# Optimizing a Trainium2 kernel written in Bass

```python
import jax, jax.numpy as jnp
from jax import lax
import numpy as np

D_MODEL = 2048
BATCH = 1
SEQ = 512
DEPTH = 1

PLE_DIM = 256
D_FF = 4 * D_MODEL
MIX_WIDTH = D_MODEL
HG_WIDTH = MIX_WIDTH // 2
HG_HEAD_DIM = 128
HG_HEADS = HG_WIDTH // HG_HEAD_DIM
GLA_WIDTH = MIX_WIDTH - HG_WIDTH
GLA_HEADS = 4
GLA_DV = GLA_WIDTH // GLA_HEADS
GLA_DK = GLA_DV // 2
GLA_KEY_WIDTH = GLA_HEADS * GLA_DK
GLA_GATE_RANK = 16
GLA_GATE_NORM = 16.0
CONV_WIDTH = 4
CHUNK = 64
EPS = 1e-6

SPLIT_POINTS = (
    HG_WIDTH,
    2 * HG_WIDTH,
    3 * HG_WIDTH,
    4 * HG_WIDTH,
    4 * HG_WIDTH + GLA_KEY_WIDTH,
    4 * HG_WIDTH + 2 * GLA_KEY_WIDTH,
    4 * HG_WIDTH + 2 * GLA_KEY_WIDTH + GLA_WIDTH,
    4 * HG_WIDTH + 2 * GLA_KEY_WIDTH + 2 * GLA_WIDTH,
)
IN_WIDTH = 4 * HG_WIDTH + 2 * GLA_KEY_WIDTH + 2 * GLA_WIDTH + GLA_GATE_RANK
CONV_CH = 2 * GLA_KEY_WIDTH + GLA_WIDTH

kernel_name = "hgrn2_gla_parallel_hybrid"

def rmsnorm(x, g):
    xf = x.astype(jnp.float32)
    y = xf * lax.rsqrt(jnp.mean(xf * xf, axis=-1, keepdims=True) + EPS)
    return (y * g.astype(jnp.float32)).astype(x.dtype)

def head_rmsnorm(o, g):
    B, S, H, dv = o.shape
    y = o * lax.rsqrt(jnp.mean(o * o, axis=-1, keepdims=True) + EPS)
    return (y * g.astype(jnp.float32).reshape(H, dv)).reshape(B, S, H * dv)

def causal_short_conv(x, w):
    S = x.shape[1]
    xp = jnp.pad(x, ((0, 0), (CONV_WIDTH - 1, 0), (0, 0)))
    return sum(xp[:, j:j + S] * w[j] for j in range(CONV_WIDTH))

def chunked_gated_recurrence(q, k, v, log_a):
    B, S, H, dk = q.shape
    dv = v.shape[-1]
    n = S // CHUNK

    def to_chunks(t):
        return t.astype(jnp.float32).reshape(B, n, CHUNK, H, t.shape[-1]).transpose(1, 0, 3, 2, 4)

    qc, kc, vc, ac = to_chunks(q), to_chunks(k), to_chunks(v), to_chunks(log_a)
    causal = jnp.tril(jnp.ones((CHUNK, CHUNK), dtype=bool))[:, :, None]

    def step(state, inp):
        qi, ki, vi, ai = inp
        b = jnp.cumsum(ai, axis=2)
        diff = b[:, :, :, None, :] - b[:, :, None, :, :]
        decay = jnp.exp(jnp.where(causal, diff, -jnp.inf))
        scores = jnp.einsum('bhtc,bhsc,bhtsc->bhts', qi, ki, decay)
        o_intra = jnp.einsum('bhts,bhsv->bhtv', scores, vi)
        o_inter = jnp.einsum('bhtc,bhcv->bhtv', qi * jnp.exp(b), state)
        b_last = b[:, :, -1:, :]
        k_dec = ki * jnp.exp(b_last - b)
        new_state = jnp.exp(b_last[:, :, 0, :])[..., None] * state + jnp.einsum('bhsc,bhsv->bhcv', k_dec, vi)
        return new_state, o_intra + o_inter

    state0 = jnp.zeros((B, H, dk, dv), jnp.float32)
    _, o = lax.scan(step, state0, (qc, kc, vc, ac))
    return o.transpose(1, 0, 3, 2, 4).reshape(B, S, H, dv)

def setup_inputs(seed: int = 0) -> dict:
    key = jax.random.key(seed)
    ks = jax.random.split(key, 24)
    f32 = jnp.float32

    def nrm(k, shape, scale):
        return jax.random.normal(k, shape, f32) * scale

    def gain(k, shape):
        return 1.0 + 0.02 * jax.random.normal(k, shape, f32)

    return {
        "x": nrm(ks[0], (BATCH, SEQ, D_MODEL), 1.0),
        "p": nrm(ks[1], (DEPTH, BATCH, SEQ, PLE_DIM), 1.0),
        "g_mix": gain(ks[2], (DEPTH, D_MODEL)),
        "w_in": nrm(ks[3], (DEPTH, D_MODEL, IN_WIDTH), D_MODEL ** -0.5),
        "lb_logits": nrm(ks[4], (DEPTH, HG_WIDTH), 1.0),
        "g_hg_norm": gain(ks[5], (DEPTH, HG_WIDTH)),
        "conv_w": nrm(ks[6], (DEPTH, CONV_WIDTH, CONV_CH), CONV_WIDTH ** -0.5),
        "w_gla_gate": nrm(ks[7], (DEPTH, GLA_GATE_RANK, GLA_KEY_WIDTH), GLA_GATE_RANK ** -0.5),
        "b_gla_gate": nrm(ks[8], (DEPTH, GLA_KEY_WIDTH), 0.1),
        "g_gla_norm": gain(ks[9], (DEPTH, GLA_WIDTH)),
        "w_out": nrm(ks[10], (DEPTH, MIX_WIDTH, D_MODEL), MIX_WIDTH ** -0.5),
        "g_mlp": gain(ks[11], (DEPTH, D_MODEL)),
        "w_up": nrm(ks[12], (DEPTH, D_MODEL, D_FF), D_MODEL ** -0.5),
        "w_down": nrm(ks[13], (DEPTH, D_FF, D_MODEL), D_FF ** -0.5),
        "g_ple": gain(ks[14], (DEPTH, D_MODEL)),
        "w_pg": nrm(ks[15], (DEPTH, D_MODEL, D_MODEL), D_MODEL ** -0.5),
        "w_pp": nrm(ks[16], (DEPTH, PLE_DIM, D_MODEL), PLE_DIM ** -0.5),
        "g_final": gain(ks[17], (D_MODEL,)),
    }

def reference(x, p, g_mix, w_in, lb_logits, g_hg_norm, conv_w, w_gla_gate, b_gla_gate,
              g_gla_norm, w_out, g_mlp, w_up, w_down, g_ple, w_pg, w_pp, g_final):
    f32 = jnp.float32
    B, S, _ = x.shape
    lb_cum = jnp.cumsum(jax.nn.softmax(lb_logits.astype(f32), axis=0), axis=0)
    h = x
    for l in range(DEPTH):
        u = rmsnorm(h, g_mix[l])
        z = u @ w_in[l]
        hq, hf, hi, hg, gq, gk, gv, gr, ga = jnp.split(z, SPLIT_POINTS, axis=-1)

        lb = lb_cum[l] - lb_cum[0]
        log_f = jnp.logaddexp(jnp.log(lb), jnp.log1p(-lb) + jax.nn.log_sigmoid(hf.astype(f32)))
        k_h = -jnp.expm1(log_f)
        hs = (B, S, HG_HEADS, HG_HEAD_DIM)
        o_h = chunked_gated_recurrence(hq.reshape(hs), k_h.reshape(hs), hi.reshape(hs), log_f.reshape(hs))
        y_h = head_rmsnorm(o_h, g_hg_norm[l]) * jax.nn.silu(hg.astype(f32))

        qkv = jax.nn.silu(causal_short_conv(jnp.concatenate([gq, gk, gv], axis=-1), conv_w[l]))
        cq, ck, cv = jnp.split(qkv, (GLA_KEY_WIDTH, 2 * GLA_KEY_WIDTH), axis=-1)
        log_alpha = jax.nn.log_sigmoid((ga @ w_gla_gate[l] + b_gla_gate[l]).astype(f32)) / GLA_GATE_NORM
        ks_ = (B, S, GLA_HEADS, GLA_DK)
        o_g = chunked_gated_recurrence((cq * GLA_DK ** -0.5).reshape(ks_), ck.reshape(ks_),
                                       cv.reshape(B, S, GLA_HEADS, GLA_DV), log_alpha.reshape(ks_))
        y_g = head_rmsnorm(o_g, g_gla_norm[l]) * jax.nn.silu(gr.astype(f32))

        y = jnp.concatenate([y_h, y_g], axis=-1).astype(h.dtype)
        h = h + y @ w_out[l]

        m = rmsnorm(h, g_mlp[l]) @ w_up[l]
        h = h + jnp.square(jax.nn.relu(m)) @ w_down[l]

        gate = jax.nn.sigmoid(rmsnorm(h, g_ple[l]) @ w_pg[l])
        h = h + gate * (p[l] @ w_pp[l])
    return rmsnorm(h, g_final)


_drawn_inputs = setup_inputs


def setup_inputs(seed=0):
    import zlib

    import numpy as np

    out = dict(_drawn_inputs(seed))
    spreads = {}
    factors = {'g_mix': 2.698,
     'g_hg_norm': 88.39,
     'w_gla_gate': 4.88,
     'b_gla_gate': 41.476,
     'g_gla_norm': 93.001,
     'g_mlp': 11.916,
     'g_ple': 200.0,
     'g_final': 22.337,
     'p': 8.0,
     'w_pg': 8.0,
     'w_pp': 8.0}
    for name, (base, spread) in spreads.items():
        noise = np.random.default_rng([zlib.crc32(name.encode()), seed]).standard_normal(out[name].shape)
        drawn = base * np.exp(spread * noise) if base else spread * noise
        out[name] = __import__('jax').numpy.asarray(drawn.astype(out[name].dtype))
    for name, factor in factors.items():
        out[name] = (out[name] * factor).astype(out[name].dtype)
    return out
```

```python
import math
from contextlib import ExitStack

import concourse.bass as bass
from concourse import mybir

F32 = mybir.dt.float32
F32R = mybir.dt.float32r
BF16 = mybir.dt.bfloat16
U8 = mybir.dt.uint8
ALU = mybir.AluOpType
ACT = mybir.ActivationFunctionType
ds = bass.ds

P = 128
S = 512
NT = S // P
D = 2048
KT = D // P
HG_HEADS, GLA_HEADS = 8, 4
HEADS = HG_HEADS + GLA_HEADS
HG_W = HG_HEADS * P
GLA_KW = GLA_HEADS * P
GLA_W = GLA_HEADS * 2 * P
RANK = 16
IN_W = 4 * HG_W + 2 * GLA_KW + 2 * GLA_W + RANK
FF = 4 * D
PLE = 256
EPS = 1e-6
GATE_NORM = 16.0
CONV = 4
LEVELS = 7
EXP_MAX = 85.0
LN_SHIFT = 62
LN_MAX = 41.0
EARLY = 3

COL_Q, COL_F, COL_I, COL_G = 0, HG_W, 2 * HG_W, 3 * HG_W
COL_GQ = 4 * HG_W
COL_GK = COL_GQ + GLA_KW
COL_GV = COL_GK + GLA_KW
COL_GR = COL_GV + GLA_W
COL_CODE = IN_W - P

HG_UNITS, GLA_UNITS = 4, 6
U_HG = 0
U_CODE = U_HG + HG_UNITS * HG_HEADS
U_GLA = U_CODE + 1
U_OUT = U_GLA + GLA_UNITS * GLA_HEADS
U_MLP = U_OUT + KT
CH = 8
CHUNKS = FF // P // CH
MLP_UNITS, MLP_RESULTS = 2 * CH, CH + KT
U_PP = U_MLP + CHUNKS * MLP_UNITS
U_PG = U_PP + 2
UNITS = U_PG + KT
R_OUT = U_OUT
R_MLP = R_OUT + KT
R_PP = R_MLP + CHUNKS * MLP_RESULTS
R_PG = R_PP + KT

V_CONV, V_MIX, V_MLP, V_PLE, V_FINAL = 0, 64, 80, 96, 112
W_HG, W_GLA, W_LB, W_BG = 0, 8, 16, 24
N_VEC2 = 28

POOL_Y = 10
SIG_V, SIG_A = 4, 3
POOL_STEPS = 9 + 4 * LEVELS + 3 + 2
LEVEL_AT = [(3, 0), (3, 256), (4, 0), (4, 256), (5, 0), (5, 256), (6, 0)]


class Head:

    def __init__(self, kind, h):
        self.gla = kind == "gla"
        self.h = h
        self.H = HG_HEADS + h if self.gla else h
        self.vt = 2 if self.gla else 1
        self.units = GLA_UNITS if self.gla else HG_UNITS
        self.late = 5 if self.gla else 4

    def before(self, per_hg, per_gla):
        return per_hg * HG_HEADS + per_gla * self.h if self.gla else per_hg * self.h

    def sigmoid(self, what, j=0):
        if self.gla:
            return 2 * HG_HEADS + GLA_UNITS * self.h + (4 if what == "gate" else 0) + j
        return 2 * self.h + (1 if what == "gate" else 0)

    def operands(self):
        return self.sigmoid("conv", 1) if self.gla else self.sigmoid("key")

    def unit(self, j):
        return Unit(U_GLA + j, GLA_UNITS, self.h) if self.gla else Unit(U_HG + j, HG_UNITS, self.h)


class Unit:

    def __init__(self, first, per=0, i=0):
        self.first, self.per, self.i = first, per, i
        self.u = first + per * i
        self.slot = first % 2
        self.turn = first // 2 + per // 2 * i

    def next(self):
        return Unit(self.first + 1, self.per, self.i)


def build(nc, x, p, g_mix, w_in, lb_logits, g_hg_norm, conv_w, w_gla_gate, b_gla_gate, g_gla_norm,
          w_out, g_mlp, w_up, w_down, g_ple, w_pg, w_pp, g_final, out):
    x_tok = x[0].rearrange("(t q) d -> q t d", q=P)
    p_tok = p[0, 0].rearrange("(t q) d -> q t d", q=P)
    out_tok = out[0].rearrange("(t q) d -> q t d", q=P)
    w_in_k = w_in[0].rearrange("(k q) n -> q k n", q=P)
    w_out_k = w_out[0].rearrange("(k q) n -> q k n", q=P)
    w_up_k = w_up[0].rearrange("(k q) n -> q k n", q=P)
    w_down_k = w_down[0].rearrange("(c k q) n -> q (c k) n", q=P, k=CH)
    w_pg_k = w_pg[0].rearrange("(k q) n -> q k n", q=P)
    w_pp_k = w_pp[0].rearrange("(k q) n -> q k n", q=P)
    xT_dram = nc.dram_tensor("xT_scratch", (KT, P, S), F32, kind="Internal").ap()

    ctx = ExitStack()
    with ctx:
        def sb(name, shape, dt=F32, stack=None):
            return (stack or ctx).enter_context(nc.sbuf_tensor(name, shape, dt))

        def sem(name):
            return ctx.enter_context(nc.semaphore(name))

        def tile(t, i):
            return t[:, ds(i, 1), :].rearrange("q o s -> q (o s)")

        u_hi = sb("u_hi", [P, KT, S], F32R)
        u_lo = sb("u_lo", [P, KT, S], F32R)
        w_raw = sb("w_raw", [P, 2, D])
        w_hi = sb("w_hi", [P, 2, D], F32R)
        w_lo = sb("w_lo", [P, 2, D], F32R)
        ident = sb("ident", [P, P])
        ones = sb("ones", [P, P])
        vec1 = sb("vec1", [P, P])
        vec2 = sb("vec2", [P, N_VEC2])
        lb_e = sb("lb_e", [P, HG_HEADS])
        lb_r = sb("lb_r", [P, HG_HEADS])
        lb = sb("lb", [P, HG_HEADS])
        minus_one_plus_lb = sb("minus_one_plus_lb", [P, HG_HEADS])
        one_col = sb("one_col", [P, 1])
        ln_scale_col = sb("ln_scale_col", [P, 1])
        ln_shift_col = sb("ln_shift_col", [P, 1])
        x_sum = sb("x_sum", [P, NT * NT])
        x_rs = sb("x_rs", [P, 3, NT])
        rs_u = sb("rs_u", [P, S])

        reg1, reg2 = ExitStack(), ExitStack()
        region1 = nc.sbuf_base
        y = sb("y", [P, KT, S], stack=reg1)
        inverse = y[:, KT - 2, :]
        code = y[:, KT - 1, :]
        w_gate = y[:, KT - 3, :]
        x_in = y[:, :, :].rearrange("q (t c) s -> q t (c s)", t=NT)

        def mx(name, shape, dt=F32):
            return sb(name, shape, dt, reg2)

        zf = mx("zf", [P, S])
        zq = mx("zq", [P, S])
        zv = mx("zv", [P, 2, S])
        kk = mx("kk", [P, S])
        b = mx("b", [P, S])
        tmp = mx("tmp", [P, 3, S])
        kl = mx("kl", [P, 4, S])
        ql = mx("ql", [P, 4, 256])
        conv_in = mx("conv_in", [P, CONV - 1 + S])
        masks = mx("masks", [P, LEVELS, 256], U8)
        mask_diag = mx("mask_diag", [P, S], U8)
        scan_mask = mx("scan_mask", [P, S], BF16)
        zg = mx("zg", [P, 2, S])
        ez = mx("ez", [P, S])
        norm = mx("norm", [P, 3, S])
        A = mx("A", [P, NT * S])
        V = mx("V", [P, NT, 2 * P])
        decay01 = mx("decay01", [P, 1])
        w_gate_h = mx("w_gate_h", [P, P])
        x_square = zg[:, 0, :]
        x_rs_diag = norm[:, 2, :]
        rows1 = norm[:, 0, 0:P]
        rows2 = norm[:, 1, 0:P]
        mask_f = V[:, 0:2, :].rearrange("q a c -> q (a c)")
        reg2.close()
        reg1.close()

        a_hi = sb("a_hi", [P, CH, S], F32R)
        a_lo = sb("a_lo", [P, CH, S], F32R)
        h = sb("h", [P, KT, S])
        p_hi = sb("p_hi", [P, 2, S], F32R)
        p_lo = sb("p_lo", [P, 2, S], F32R)
        relu = sb("relu", [P, 2, S])
        p_in = relu[:, :, :].rearrange("q a (c d) -> q (a c) d", d=PLE)
        work = sb("work", [P, 2, S])
        norm2 = sb("norm2", [P, 3, S])
        pp = nc.alloc_sbuf_tensor_at("pp", [P, KT, S], F32, offset=region1)
        sum_sq = sb("sum_sq", [P, S])
        sq_tmp = sb("sq_tmp", [P, S])
        tok = sb("tok", [P, 3, NT])

        bank = [ctx.enter_context(nc.psum_tensor(f"bank{i}", [P, S], F32)) for i in range(8)]

        rows_landed, gate_landed, p_landed = sem("rows_landed"), sem("gate_landed"), sem("p_landed")
        x_landed = [sem(f"x_landed{c}") for c in range(NT)]
        xT_stored = [sem(f"xT_stored{c}") for c in range(4)]
        h_landed = [sem(f"h_landed{c}") for c in range(KT // 4)]
        out_stored = sem("out_stored")
        raw_landed = [sem("raw_landed0"), sem("raw_landed1")]
        pool_step, vec_ps, vec_ready, lb_step, lb_exp = (
            sem("pool_step"), sem("vec_ps"), sem("vec_ready"), sem("lb_step"), sem("lb_exp"))
        w_hi_ready, w_lo_ready = sem("w_hi_ready"), sem("w_lo_ready")
        z_done, z_evac = sem("z_done"), sem("z_evac")
        u_hi_ready, u_lo_ready = sem("u_hi_ready"), sem("u_lo_ready")
        y_lo_ready = sem("y_lo_ready")
        u_read = sem("u_read")
        xT_ps, xT_copied, sq_done, sum_done = sem("xT_ps"), sem("xT_copied"), sem("sq_done"), sem("sum_done")
        x_squared, x_stat_step, x_stat_act = sem("x_squared"), sem("x_stat_step"), sem("x_stat_act")
        diag_ready, last_squared = sem("diag_ready"), sem("last_squared")
        stat_ps, stat_step, stat_act = sem("stat_ps"), sem("stat_step"), sem("stat_act")
        decay_act, decay_step = sem("decay_act"), sem("decay_step")
        b_ready = sem("b_ready")
        sig_step, sig_act = sem("sig_step"), sem("sig_act")
        gate_zeroed, alpha_w, alpha_ps, conv_step = (
            sem("gate_zeroed"), sem("alpha_w"), sem("alpha_ps"), sem("conv_step"))
        diff_ready, exp_ready, level_ready = sem("diff_ready"), sem("exp_ready"), sem("level_ready")
        diag_done, scores_done, cross_done, vT_done = (
            sem("diag_done"), sem("scores_done"), sem("cross_done"), sem("vT_done"))
        diag_placed, level_placed, cross_placed, v_placed = (
            sem("diag_placed"), sem("level_placed"), sem("cross_placed"), sem("v_placed"))
        decay01_ready, cross_exp, cross_ready = sem("decay01_ready"), sem("cross_exp"), sem("cross_ready")
        o_done, osq_act, osq_ready, osq_ready_hg, norm_ps = (
            sem("o_done"), sem("osq_act"), sem("osq_ready"), sem("osq_ready_hg"), sem("norm_ps"))
        norm_step, norm_act = sem("norm_step"), sem("norm_act")
        y_step, y_ready = sem("y_step"), sem("y_ready")
        a_hi_ready, a_lo_ready = sem("a_hi_ready"), sem("a_lo_ready")
        p_hi_ready, p_lo_ready = sem("p_hi_ready"), sem("p_lo_ready")
        pg_step, pg_act, hg_ready, turned, outT_placed = (
            sem("pg_step"), sem("pg_act"), sem("hg_ready"), sem("turned"), sem("outT_placed"))
        tok_step, tok_act, tok_scaled, tok_scaled_act = (
            sem("tok_step"), sem("tok_act"), sem("tok_scaled"), sem("tok_scaled_act"))

        def right(t, lv):
            return t.rearrange("q (n c) -> q n c", c=2 << lv)[:, :, 1 << lv:2 << lv]

        def left(t, lv):
            return t.rearrange("q (n c) -> q n c", c=2 << lv)[:, :, 0:1 << lv]

        def halves(t, lv):
            return t.rearrange("q (n c) -> q n c", c=1 << lv)

        def diag_blocks(lv=None):
            v = A[:, :].rearrange("q (i c) -> q i c", c=512)[:, :, 0:P]
            if lv is None:
                return v
            return v.rearrange("q i (n c) -> q i n c", c=2 << lv)[:, :, :, 1 << lv:2 << lv]

        def row(v, i):
            return v[:, i * P:(i + 1) * P]

        def load_rows(engine, half):
            groups = [(rows1, V_CONV, 64, conv_w[0].rearrange("j (c q) -> (j c) q", q=P))]
            groups += [(rows1, at, KT, g.rearrange("(c q) -> c q", q=P))
                       for at, g in ((V_MIX, g_mix[0]), (V_MLP, g_mlp[0]), (V_PLE, g_ple[0]), (V_FINAL, g_final))]
            groups += [(rows2, at, n, g.rearrange("(c q) -> c q", q=P))
                       for at, n, g in ((W_HG, 8, g_hg_norm[0]), (W_GLA, 8, g_gla_norm[0]), (W_LB, 8, lb_logits[0]),
                                        (W_BG, 4, b_gla_gate[0]))]
            for rows, at, n, src in groups[half::2]:
                engine.dma_start(rows[at:at + n, :], src).then_inc(rows_landed, 16)

        block = ctx.enter_context(nc.Block())

        @block.sync
        def _(sp):
            def load_x(c):
                sp.dma_start(x_in[:, :, c * S:(c + 1) * S], x_tok[:, :, c * S:(c + 1) * S]).then_inc(x_landed[c], 16)

            def load(unit, src, k, at=0):
                if not isinstance(at, int):
                    sp.compute_val(at * 4)
                if not isinstance(unit.u, int) or unit.u >= 2:
                    sp.wait_ge(w_lo_ready, unit.u - 1)
                sp.dma_start(w_raw[:, unit.slot, :].rearrange("q (k m) -> q k m", k=k), src)\
                    .then_inc(raw_landed[unit.slot], 16)

            def load_hg(hd, j):
                col = (COL_F, COL_Q, COL_I, COL_G)[j] + hd.h * P
                load(hd.unit(j), w_in_k[:, :, ds(col, P)], KT, col)

            def load_square(first, w, i, j):
                col = (2 * i + j) * P
                load(Unit(first + j, 2, i), w[:, :, ds(col, P)], KT, col)

            first = Head("hg", 0)
            load_rows(sp, 0)
            load_x(0)
            load_hg(first, 0)
            for c in range(1, NT):
                load_x(c)
            load_hg(first, 1)
            for c in range(KT // 4):
                sp.wait_ge(xT_copied, 4 * c + 4)
                sp.dma_start(xT_dram[4 * c:4 * c + 4].rearrange("k q s -> q k s"), h[:, 4 * c:4 * c + 4, :])\
                    .then_inc(xT_stored[c], 16)
            sp.wait_ge(gate_zeroed, 1)
            sp.dma_start(w_gate[P - RANK:P, :], w_gla_gate[0]).then_inc(gate_landed, 16)
            load_hg(first, 2)
            load_hg(first, 3)
            with sp.Fori(1, HG_HEADS) as i:
                for j in range(HG_UNITS):
                    load_hg(Head("hg", i), j)
            load(Unit(U_CODE), w_in_k[:, :, COL_CODE:IN_W], KT)
            with sp.Fori(0, GLA_HEADS) as i:
                hd = Head("gla", i)
                for j, col in enumerate((COL_GK + i * P, COL_GQ + i * P, COL_GV + i * 2 * P, COL_GV + i * 2 * P + P,
                                         COL_GR + i * 2 * P, COL_GR + i * 2 * P + P)):
                    load(hd.unit(j), w_in_k[:, :, ds(col, P)], KT, col)
            for m in range(3):
                load_square(U_OUT, w_out_k, m // 2, m % 2)
            sp.wait_ge(vT_done, HEADS)
            for c in range(KT // 4):
                sp.wait_ge(xT_stored[c], 16)
                sp.dma_start(h[:, 4 * c:4 * c + 4, :], xT_dram[4 * c:4 * c + 4].rearrange("k q s -> q k s"))\
                    .then_inc(h_landed[c], 16)
            load_square(U_OUT, w_out_k, 1, 1)
            sp.wait_ge(y_ready, HEADS)
            sp.dma_start(p_in[:, :, :], p_tok).then_inc(p_landed, 16)
            with sp.Fori(2, KT // 2) as i:
                for j in range(2):
                    load_square(U_OUT, w_out_k, i, j)
            with sp.Fori(0, CHUNKS) as c:
                for j in range(CH):
                    load(Unit(U_MLP + j, MLP_UNITS, c), w_up_k[:, :, ds(c * CH * P + j * P, P)], KT,
                         c * CH * P + j * P)
                for j in range(CH):
                    load(Unit(U_MLP + CH + j, MLP_UNITS, c),
                         w_down_k[:, ds(c * CH, CH), 2 * j * P:2 * (j + 1) * P], CH)
            for j in range(2):
                load(Unit(U_PP + j), w_pp_k[:, :, j * D // 2:(j + 1) * D // 2], 2)
            with sp.Fori(0, KT // 2) as i:
                for j in range(2):
                    load_square(U_PG, w_pg_k, i, j)
            for t in (0, 3, 1, 2):
                if t == NT - 1:
                    sp.wait_ge(tok_scaled_act, 1)
                else:
                    sp.wait_ge(tok_scaled, t + 1)
                sp.dma_start(out_tok[:, t, :].rearrange("q (m f) -> q m f", m=KT),
                             h[:, :, t * P:(t + 1) * P]).then_inc(out_stored, 16)
            sp.wait_ge(out_stored, 16 * NT)

        @block.gpsimd
        def _(pool):
            def split_lo(unit):
                pool.wait_ge(w_hi_ready, unit.u + 1)
                pool.wait_ge(w_lo_ready, unit.u)
                pool.tensor_tensor(w_lo[:, unit.slot, :], w_raw[:, unit.slot, :],
                                   w_hi[:, unit.slot, :].bitcast(F32), ALU.subtract).then_inc(w_lo_ready, 1)

            pool.memset(ident[:], 0.0).then_inc(pool_step, 1)
            pool.wait_ge(pool_step, 1)
            pool.affine_select(out=ident[:], in_=ident[:], compare_op=ALU.not_equal, fill=1.0, base=0,
                               pattern=[[-1, P]], channel_multiplier=1).then_inc(pool_step, 1)
            pool.memset(ones[:], 1.0).then_inc(pool_step, 1)
            pool.memset(one_col[:], 1.0).then_inc(pool_step, 1)
            pool.memset(A[:], 0.0).then_inc(pool_step, 1)
            pool.memset(ln_scale_col[:], 2.0 ** -LN_SHIFT).then_inc(pool_step, 1)
            pool.memset(ln_shift_col[:], -LN_SHIFT * math.log(2.0)).then_inc(pool_step, 1)
            pool.memset(scan_mask[:], 1.0).then_inc(pool_step, 1)
            pool.wait_ge(pool_step, 8)
            pool.memset(scan_mask[:, :].rearrange("q (t c) -> q t c", c=P)[:, :, 0:1], 0.0).then_inc(pool_step, 1)
            step = 9
            for lv in range(LEVELS + 1):
                diagonal = lv == LEVELS
                half = P if diagonal else 1 << lv
                n = P // (half if diagonal else 2 * half)
                width = S if diagonal else 256
                m = mask_f[:, 0:width]
                pool.wait_ge(pool_step, step)
                pool.memset(m, 1.0).then_inc(pool_step, 1)
                pool.wait_ge(pool_step, step + 1)
                if diagonal:
                    pool.affine_select(out=m, in_=m, compare_op=ALU.is_equal, fill=0.0, base=0,
                                       pattern=[[0, NT], [-1, P]], channel_multiplier=1).then_inc(pool_step, 1)
                    pool.wait_ge(pool_step, step + 2)
                    pool.tensor_copy(mask_diag[:], m).then_inc(pool_step, 1)
                    step += 3
                    continue
                pool.affine_select(out=m, in_=m, compare_op=ALU.is_ge, fill=0.0, base=0,
                                   pattern=[[0, NT], [-2 * half, n], [0, half]], channel_multiplier=1)\
                    .then_inc(pool_step, 1)
                pool.wait_ge(pool_step, step + 2)
                pool.affine_select(out=m, in_=m, compare_op=ALU.is_ge, fill=0.0, base=half - 1,
                                   pattern=[[0, NT], [2 * half, n], [0, half]], channel_multiplier=-1)\
                    .then_inc(pool_step, 1)
                pool.wait_ge(pool_step, step + 3)
                pool.tensor_copy(masks[:, lv, :], m).then_inc(pool_step, 1)
                step += 4
                if lv == 2:
                    split_lo(Unit(1))
            pool.wait_ge(xT_stored[KT // 4 - 1], 16)
            pool.wait_ge(u_lo_ready, KT)
            pool.memset(conv_in[:, 0:CONV - 1], 0.0).then_inc(pool_step, 1)
            pool.wait_ge(xT_stored[KT // 4 - 2], 16)
            pool.memset(kl[:], 0.0).then_inc(pool_step, 1)
            assert step + 2 == POOL_STEPS
            pool.wait_ge(xT_ps, KT)
            pool.wait_ge(x_squared, NT * NT)
            pool.memset(w_gate, 0.0).then_inc(gate_zeroed, 1)

            def gate_weights(hd):
                pool.wait_ge(alpha_ps, hd.h)
                pool.tensor_copy(w_gate_h[:], w_gate[:, ds(hd.h * P, P)]).then_inc(alpha_w, 1)

            def differences(hd):
                for lv in range(LEVELS):
                    if hd.gla and lv == EARLY + 2:
                        split_lo(hd.unit(5))
                    if lv == 0:
                        pool.wait_ge(b_ready, hd.H + 1)
                        pool.wait_ge(level_ready, LEVELS * hd.H)
                        pool.wait_ge(cross_done, hd.H)
                    elif lv == 1:
                        pass
                    else:
                        pool.wait_ge(level_ready, LEVELS * hd.H + lv - 1)
                    bv = b[:, :].rearrange("q (n c) -> q n c", c=2 << lv)
                    ref = bv[:, :, (1 << lv) - 1:1 << lv].to_broadcast([P, S // (2 << lv), 2 << lv])
                    pool.tensor_tensor(tmp[:, lv % 2, :].rearrange("q (n c) -> q n c", c=2 << lv), bv, ref,
                                       ALU.subtract).then_inc(diff_ready, 1)

            def square_sum(hd):
                pool.wait_ge(osq_act, 2 * hd.h + 2)
                pool.tensor_tensor(norm[:, 0, :], norm[:, 0, :], norm[:, 1, :], ALU.add).then_inc(osq_ready, 1)

            first = Head("hg", 0)
            differences(first)
            with pool.Fori(1, HG_HEADS) as i:
                differences(Head("hg", i))
            pool.wait_ge(gate_landed, 16)
            gate_weights(Head("gla", 0))
            differences(Head("gla", 0))
            with pool.Fori(1, GLA_HEADS) as i:
                gate_weights(Head("gla", i))
                square_sum(Head("gla", i - 1))
                differences(Head("gla", i))
            for k in range(POOL_Y):
                pool.wait_ge(u_hi_ready, KT + k + 1)
                pool.tensor_tensor(u_lo[:, k, :], y[:, k, :], u_hi[:, k, :].bitcast(F32), ALU.subtract)\
                    .then_inc(u_lo_ready, 1)

            def accumulate(n, t, i, ready, count):
                pool.wait_ge(ready, count)
                pool.tensor_tensor(sq_tmp[:], t, t, ALU.mult).then_inc(sq_done, 1)
                pool.wait_ge(sq_done, n * KT + i + 1)
                pool.tensor_tensor(sum_sq[:], sum_sq[:], sq_tmp[:], ALU.add).then_inc(sum_done, 1)

            for n, (ready, base) in enumerate(((z_evac, R_OUT), (z_evac, R_MLP + (CHUNKS - 1) * MLP_RESULTS + CH),
                                               (pg_step, 0))):
                per = 5 if n == 2 else 1
                if n == 0:
                    pool.wait_ge(y_ready, HEADS)
                else:
                    pool.wait_ge(stat_ps, n + 1)
                    pool.wait_ge(sum_done, (KT + 1) * n)
                pool.memset(sum_sq[:], 0.0).then_inc(sum_done, 1)
                with pool.Fori(0, KT - 1 if n == 2 else KT) as i:
                    pool.wait_ge(sum_done, (KT + 1) * n + 1 + i)
                    accumulate(n, tile(h, i), i, ready, base + (i + 1) * per)

        @block.scalar
        def _(act):
            load_rows(act, 1)
            act.preload_act_table_set("natural_log_exp_and_others")

            def split_hi(unit, done):
                if not isinstance(done, int) or done > 0:
                    act.wait_ge(z_done, done)
                act.wait_ge(raw_landed[unit.slot], 16 * unit.turn + 16)
                act.activation(w_hi[:, unit.slot, :], w_raw[:, unit.slot, :], ACT.Copy).then_inc(w_hi_ready, 1)

            def rms_ln_exp(buf, step, count, done, n):
                act.wait_ge(step, count)
                act.activation(buf[1], buf[0], ACT.Ln).then_inc(done, 1)
                act.wait_ge(done, n + 1)
                act.activation(buf[1], buf[1], ACT.Exp, scale=-0.5).then_inc(done, 1)

            def soft_part(n):
                act.activation(tmp[:, 1, :], zf[:], ACT.Abs).then_inc(decay_act, 1)
                act.wait_ge(decay_act, n + 1)
                act.activation(tmp[:, 1, :], tmp[:, 1, :], ACT.Exp, scale=-1.0).then_inc(decay_act, 1)
                act.wait_ge(decay_act, n + 2)
                act.activation(tmp[:, 1, :], tmp[:, 1, :], ACT.Ln, bias=one_col[:, :]).then_inc(decay_act, 1)

            def inverse_1_plus_exp(n, scale, src=None):
                act.activation(ez[:], ez[:] if src is None else src, ACT.Exp, scale=scale).then_inc(sig_act, 1)
                act.wait_ge(sig_act, SIG_A * n + 1)
                act.activation(inverse, ez[:], ACT.Ln, bias=ln_scale_col[:, :], scale=2.0 ** -LN_SHIFT)\
                    .then_inc(sig_act, 1)
                act.wait_ge(sig_act, SIG_A * n + 2)
                act.activation(inverse, inverse, ACT.Exp, bias=ln_shift_col[:, :], scale=-1.0).then_inc(sig_act, 1)

            def forget_gate(hd):
                n = hd.before(5, 3)
                act.wait_ge(sig_step, SIG_V * hd.sigmoid("key") + 1)
                act.activation(tmp[:, 2, :], tmp[:, 0, :], ACT.Exp, scale=-1.0).then_inc(decay_act, 1)
                inverse_1_plus_exp(hd.sigmoid("key"), 1.0, tmp[:, 0, :])
                soft_part(n + 1)
                act.activation(tmp[:, 2, :], tmp[:, 2, :], ACT.Ln, bias=one_col[:, :],
                               scale=lb[:, ds(hd.h, 1)]).then_inc(decay_act, 1)

            def alpha(hd):
                act.wait_ge(decay_step, hd.before(2, 3) + 1)
                soft_part(hd.before(5, 3))

            def silu(hd, what, j=0):
                n = hd.sigmoid(what, j)
                act.wait_ge(sig_step, SIG_V * n + 1)
                inverse_1_plus_exp(n, -1.0)

            def level_exps(hd, levels):
                for lv in levels:
                    d = tmp[:, lv % 2, :]
                    act.wait_ge(diff_ready, LEVELS * hd.H + lv + 1)
                    act.activation(left(d, lv), left(d, lv), ACT.Exp, scale=-1.0)
                    act.activation(right(d, lv), right(d, lv), ACT.Exp).then_inc(exp_ready, 1)

            def cross_exps(hd):
                act.wait_ge(decay01_ready, hd.H + 1)
                kd, qd = tmp[:, 2, :], tmp[:, 0, :]
                for t in range(3):
                    act.activation(row(kd, t), row(b, t), ACT.Exp, scale=-1.0, bias=b[:, t * P + P - 1:t * P + P])
                act.activation(row(kd, 3), row(b, 0), ACT.Exp, scale=-1.0, bias=decay01[:, :])
                act.activation(qd[:, 0:2 * P], b[:, P:3 * P], ACT.Exp)
                act.activation(row(qd, 2), row(b, 3), ACT.Exp, bias=b[:, 3 * P - 1:3 * P])
                act.activation(row(qd, 3), row(b, 3), ACT.Exp).then_inc(cross_exp, 1)

            def place_cross(hd):
                act.wait_ge(cross_done, hd.H + 1)
                act.wait_ge(level_placed, LEVELS * (hd.H + 1))
                act.wait_ge(o_done, hd.H)
                act.activation(A[:, P:2 * P], bank[6][:, 2 * P:3 * P], ACT.Copy)
                act.activation(A[:, 9 * P:10 * P], bank[6][:, 3 * P:4 * P], ACT.Copy)
                act.activation(A[:, 2 * P:4 * P], bank[7][:, 0:2 * P], ACT.Copy)
                act.activation(A[:, 5 * P:7 * P], bank[7][:, 2 * P:4 * P], ACT.Copy).then_inc(cross_placed, 1)

            def place_values(hd):
                act.wait_ge(vT_done, hd.H + 1)
                for v in range(hd.vt):
                    last = act.activation(V[:, :, v * P:(v + 1) * P],
                                          bank[2 + v][:, :].rearrange("q (t c) -> q t c", c=P), ACT.Copy)
                last.then_inc(v_placed, 1)

            def output_gates(hd):
                for v in range(hd.vt):
                    silu(hd, "gate", v)

            def square_o(hd):
                act.wait_ge(o_done, hd.H + 1)
                act.wait_ge(y_ready, hd.H)
                for v in range(hd.vt):
                    act.activation(norm[:, v, :], bank[2 + 2 * v][:, :], ACT.Square)\
                        .then_inc(osq_act if hd.gla else osq_ready_hg, 1)

            def head_norm(hd):
                rms_ln_exp((norm[:, 0, :], norm[:, 1, :]), norm_step, 5 * hd.H + 1, norm_act, 2 * hd.H)

            def iteration(hd, prev):
                def slot(j):
                    split_hi(hd.unit(j + 1), hd.unit(j).u)

                if prev:
                    slot(0)
                    place_cross(prev)
                    place_values(prev)
                    output_gates(prev)
                slot(1)
                if prev:
                    square_o(prev)
                if hd.gla:
                    alpha(hd)
                    silu(hd, "conv", 0)
                else:
                    forget_gate(hd)
                slot(2)
                if prev:
                    head_norm(prev)
                if hd.gla:
                    silu(hd, "conv", 1)
                    slot(3)
                level_exps(hd, range(EARLY + 1))
                if hd.gla:
                    silu(hd, "conv", 2)
                slot(hd.late - 1)
                if hd.gla:
                    silu(hd, "conv", 3)
                level_exps(hd, range(EARLY + 1, LEVELS))
                cross_exps(hd)
                if hd.gla:
                    slot(5)

            act.wait_ge(vec_ready, 1)
            for k in range(KT):
                act.wait_ge(xT_copied, k + 1)
                act.activation(u_hi[:, k, :], h[:, k, :], ACT.Identity,
                               scale=vec1[:, V_MIX + k:V_MIX + k + 1]).then_inc(u_hi_ready, 1)
                if k == 10:
                    split_hi(Unit(1), 0)
                if k == 2:
                    act.wait_ge(lb_step, 1)
                    act.activation(lb_e[:], lb_e[:], ACT.Exp).then_inc(lb_exp, 1)
                c, t = k // NT, k % NT
                act.wait_ge(x_landed[c], 16)
                if k:
                    act.wait_ge(x_squared, k)
                act.activation(x_square, x_in[:, t, c * S:(c + 1) * S], ACT.Square,
                               accum_out=x_sum[:, k:k + 1]).then_inc(x_squared, 1)
                if k == 0:
                    split_hi(Unit(0), 0)
            rms_ln_exp([x_rs[:, i, :] for i in range(3)], x_stat_step, 3, x_stat_act, 0)
            act.wait_ge(lb_step, 5)
            iteration(Head("hg", 0), None)
            with act.Fori(1, HG_HEADS) as i:
                iteration(Head("hg", i), Head("hg", i - 1))
            split_hi(Unit(U_CODE + 1), U_CODE)
            iteration(Head("gla", 0), Head("hg", HG_HEADS - 1))
            with act.Fori(1, GLA_HEADS) as i:
                iteration(Head("gla", i), Head("gla", i - 1))

            last = Head("gla", GLA_HEADS - 1)

            def split_y(tiles):
                for k in tiles:
                    act.activation(u_hi[:, k, :], y[:, k, :], ACT.Copy).then_inc(u_hi_ready, 1)

            act.wait_ge(y_ready, HEADS - 1)
            def split_y_read(tiles):
                for k in tiles:
                    act.wait_ge(u_read, (KT - 1) * (GLA_HEADS - 1) + k + 1)
                    split_y([k])

            split_y_read(range(6))
            place_cross(last)
            place_values(last)
            silu(last, "gate", 0)
            split_y_read(range(6, 10))
            silu(last, "gate", 1)
            split_y_read(range(10, KT - 2))
            square_o(last)
            split_hi(Unit(U_OUT + 1), U_OUT)
            head_norm(last)
            act.wait_ge(y_ready, HEADS)
            act.wait_ge(z_done, U_OUT)
            split_y(range(KT - 2, KT))
            split_hi(Unit(U_OUT + 2), U_OUT + 1)
            with act.Fori(1, KT // 2) as i:
                for j in range(2):
                    unit = Unit(U_OUT + j, 2, i)
                    split_hi(unit.next(), unit.u)

            def split_h(k, at):
                act.activation(u_hi[:, k, :], h[:, k, :], ACT.Identity, scale=vec1[:, at + k:at + k + 1])\
                    .then_inc(u_hi_ready, 1)

            for k in range(KT):
                if k < KT - 1:
                    act.wait_ge(u_read, (KT - 1) * (GLA_HEADS + KT // 2 - 2) + k + 1)
                if k == 0:
                    act.wait_ge(z_evac, R_MLP - 1)
                if k == KT - 1:
                    act.wait_ge(z_evac, R_MLP)
                split_h(k, V_MLP)
            act.wait_ge(turned, 1)
            for f in range(2):
                act.activation(p_hi[:, f, :], bank[3 + f][:, :], ACT.Copy).then_inc(p_hi_ready, 1)

            def mlp_chunk(c, first=False, final=False):
                for j in range(CH):
                    split_hi(Unit(U_MLP + j + 1, MLP_UNITS, c), R_MLP + MLP_RESULTS * c + j)
                    if first and j == 0:
                        rms_ln_exp((norm2[:, 0, :], norm2[:, 1, :]), stat_step, 1, stat_act, 0)
                    if j >= 2:
                        act.wait_ge(a_lo_ready, CH * c + j - 1)
                    act.wait_ge(z_evac, R_MLP + j + 1 + MLP_RESULTS * c)
                    act.activation(work[:, j % 2, :], relu[:, j % 2, :], ACT.Square)
                    act.activation(a_hi[:, j, :], relu[:, j % 2, :], ACT.Square).then_inc(a_hi_ready, 1)
                for j in range(CH):
                    split_hi(Unit(U_MLP + CH + j + 1, MLP_UNITS, c), R_MLP + MLP_RESULTS * c + CH + 2 * j)
                    if final and j:
                        act.wait_ge(z_evac, R_PP - KT + 2 * j)
                        split_h(2 * j - 2, V_PLE)
                        split_h(2 * j - 1, V_PLE)

            mlp_chunk(0, first=True)
            with act.Fori(1, CHUNKS - 1) as c:
                mlp_chunk(c)
            mlp_chunk(CHUNKS - 1, final=True)
            act.wait_ge(z_evac, R_PP)
            split_h(KT - 2, V_PLE)
            split_h(KT - 1, V_PLE)
            split_hi(Unit(U_PP + 1), R_PP)
            split_hi(Unit(U_PP + 2), R_PP + KT // 2)
            rms_ln_exp((norm2[:, 0, :], norm2[:, 1, :]), stat_step, 6, stat_act, 2)

            def place_output(slot, m):
                act.wait_ge(turned, m + 2)
                if isinstance(m, int) and m == KT - 1:
                    act.wait_ge(last_squared, 1)
                else:
                    act.wait_ge(sq_done, 2 * KT + m + 1)
                act.activation(tile(h, m), bank[3 + slot][:, :], ACT.Copy).then_inc(outT_placed, 1)

            def gate_slot(unit, m, split=True):
                if split:
                    split_hi(unit.next(), R_PG + m)
                act.wait_ge(pg_step, 5 * m + 1)
                act.activation(work[:, 0, :], work[:, 0, :], ACT.Exp, scale=-1.0).then_inc(pg_act, 1)
                act.wait_ge(pg_act, 3 * m + 1)
                act.activation(relu[:, 0, :], work[:, 0, :], ACT.Ln, bias=ln_scale_col[:, :],
                               scale=2.0 ** -LN_SHIFT).then_inc(pg_act, 1)
                act.wait_ge(pg_act, 3 * m + 2)
                act.activation(relu[:, 0, :], relu[:, 0, :], ACT.Exp, bias=ln_shift_col[:, :], scale=-1.0)\
                    .then_inc(pg_act, 1)

            gate_slot(Unit(U_PG), 0)
            with act.Fori(0, KT // 2 - 1) as i:
                for j in range(1, 3):
                    gate_slot(Unit(U_PG + j, 2, i), 2 * i + j)
                    place_output((U_PG + j - 1) % 2, 2 * i + (j - 1))
            gate_slot(Unit(UNITS - 1), KT - 1, False)
            place_output((UNITS - 2) % 2, KT - 2)
            act.wait_ge(pg_step, 5 * KT)
            act.activation(relu[:, 1, :], h[:, KT - 1, :], ACT.Square).then_inc(last_squared, 1)
            place_output((UNITS - 1) % 2, KT - 1)
            rms_ln_exp((tok[:, 0, :], tok[:, 1, :]), tok_step, 1, tok_act, 0)
            act.wait_ge(tok_step, 5)
            t = NT - 1
            act.activation(h[:, :, t * P:(t + 1) * P], h[:, :, t * P:(t + 1) * P], ACT.Copy,
                           scale=tok[:, 1, t:t + 1]).then_inc(tok_scaled_act, 1)

        @block.vector
        def _(v):
            def split_lo(unit):
                v.wait_ge(w_hi_ready, unit.u + 1)
                v.tensor_tensor(w_lo[:, unit.slot, :], w_raw[:, unit.slot, :],
                                w_hi[:, unit.slot, :].bitcast(F32), ALU.subtract).then_inc(w_lo_ready, 1)

            def evacuate(unit, dst):
                v.wait_ge(z_done, unit.u + 1)
                v.tensor_tensor(dst, bank[unit.slot][:, :], rs_u[:], ALU.mult).then_inc(z_evac, 1)

            def mean_square(buf, ps, n, step):
                v.tensor_scalar(buf[0], ps, 1.0 / n, EPS, ALU.mult, ALU.add).then_inc(step, 1)

            def refine(buf, out_, step, n, done, count):
                v.wait_ge(done, count)
                v.tensor_tensor(buf[2], buf[1], buf[1], ALU.mult).then_inc(step, 1)
                v.wait_ge(step, n + 1)
                v.tensor_tensor(buf[2], buf[2], buf[0], ALU.mult).then_inc(step, 1)
                v.wait_ge(step, n + 2)
                v.tensor_scalar(buf[2], buf[2], -0.5, 1.5, ALU.mult, ALU.add).then_inc(step, 1)
                v.wait_ge(step, n + 3)
                v.tensor_tensor(out_, buf[1], buf[2], ALU.mult).then_inc(step, 1)

            norm_bufs = [norm[:, i, :] for i in range(3)]
            norm2_bufs = [norm2[:, i, :] for i in range(3)]

            def stream_mean(n, bufs):
                v.wait_ge(stat_ps, n + 1)
                mean_square(bufs, bank[2][:, :], D, stat_step)

            def stream_refine(n, bufs):
                refine(bufs, rs_u[:], stat_step, 5 * (n - 1) + 1, stat_act, 2 * (n - 1) + 2)

            def refine_inverse(n):
                v.wait_ge(sig_act, SIG_A * n + SIG_A)
                v.scalar_tensor_tensor(out=ez[:], in0=ez[:], scalar=1.0, in1=inverse, op0=ALU.add, op1=ALU.mult)\
                    .then_inc(sig_step, 1)
                v.wait_ge(sig_step, SIG_V * n + 2)
                v.scalar_tensor_tensor(out=inverse, in0=ez[:], scalar=2.0, in1=inverse, op0=ALU.subtract,
                                       op1=ALU.mult).then_inc(sig_step, 1)
                v.wait_ge(sig_step, SIG_V * n + 3)

            def clamp(hd, what, j, z):
                n = hd.sigmoid(what, j)
                v.wait_ge(sig_step, SIG_V * n)
                v.tensor_scalar(ez[:], z, -EXP_MAX, None, ALU.max).then_inc(sig_step, 1)

            def apply_silu(hd, what, j, z, scale=1.0):
                refine_inverse(hd.sigmoid(what, j))
                v.scalar_tensor_tensor(out=z, in0=z, scalar=-scale, in1=inverse, op0=ALU.mult, op1=ALU.mult)\
                    .then_inc(sig_step, 1)

            def forget_gate(hd):
                v.wait_ge(z_evac, hd.unit(0).u + 1)
                v.wait_ge(cross_done, hd.H)
                v.wait_ge(sig_step, SIG_V * hd.sigmoid("key"))
                v.tensor_scalar(tmp[:, 0, :], zf[:], -LN_MAX, EXP_MAX, ALU.max, ALU.min).then_inc(sig_step, 1)
                n = hd.sigmoid("key")
                refine_inverse(n)
                v.tensor_scalar(kk[:], inverse, minus_one_plus_lb[:, ds(hd.h, 1)], None, ALU.mult)\
                    .then_inc(sig_step, 1)
                v.wait_ge(decay_act, hd.before(5, 3) + 5)
                v.scalar_tensor_tensor(out=zf[:], in0=zf[:], scalar=0.0, in1=tmp[:, 1, :],
                                       op0=ALU.min, op1=ALU.subtract).then_inc(decay_step, 1)
                v.wait_ge(decay_step, 2 * hd.h + 1)
                v.tensor_tensor(zf[:], zf[:], tmp[:, 2, :], ALU.add).then_inc(decay_step, 1)
                v.wait_ge(decay_step, 2 * hd.h + 2)
                v.tensor_tensor_scan(b[:], scan_mask[:], zf[:], 0.0, ALU.mult, ALU.add).then_inc(b_ready, 1)

            def alpha_in(hd):
                v.wait_ge(alpha_ps, hd.h + 1)
                v.tensor_scalar(zf[:], bank[5][:, :], vec2[:, ds(hd.h + W_BG, 1)], None, ALU.add)\
                    .then_inc(decay_step, 1)

            def alpha_out(hd):
                v.wait_ge(decay_act, hd.before(5, 3) + 3)
                v.scalar_tensor_tensor(out=zf[:], in0=zf[:], scalar=0.0, in1=tmp[:, 1, :],
                                       op0=ALU.min, op1=ALU.subtract).then_inc(decay_step, 1)
                v.wait_ge(decay_step, hd.before(2, 3) + 2)
                v.tensor_scalar(zf[:], zf[:], 1.0 / GATE_NORM, None, ALU.mult).then_inc(decay_step, 1)
                v.wait_ge(decay_step, hd.before(2, 3) + 3)
                v.tensor_tensor_scan(b[:], scan_mask[:], zf[:], 0.0, ALU.mult, ALU.add).then_inc(b_ready, 1)

            def conv(hd, i, dst, ct):
                n = (4 * hd.h + i) * 4
                tap = lambda j: vec1[:, ds(ct + V_CONV + 16 * j, 1)]
                v.wait_ge(z_evac, hd.unit((0, 1, 2, 3)[i]).u + 1)
                v.tensor_scalar(dst, conv_in[:, CONV - 1:CONV - 1 + S], tap(CONV - 1), None, ALU.mult)\
                    .then_inc(conv_step, 1)
                for j in range(CONV - 1):
                    v.wait_ge(conv_step, n + j + 1)
                    v.scalar_tensor_tensor(out=dst, in0=conv_in[:, j:j + S], scalar=tap(j), in1=dst,
                                           op0=ALU.mult, op1=ALU.add).then_inc(conv_step, 1)
                v.wait_ge(conv_step, n + CONV)
                clamp(hd, "conv", i, dst)

            def level_products(hd, levels):
                for lv in levels:
                    L = LEVELS * hd.H + lv
                    d = tmp[:, lv % 2, :]
                    v.wait_ge(exp_ready, L + 1)
                    if lv >= 4:
                        v.wait_ge(scores_done, L - 3)
                    v.tensor_tensor(left(kl[:, lv % 4, :], lv), left(kk[:, :], lv), left(d, lv), ALU.mult)
                    v.tensor_tensor(halves(ql[:, lv % 4, :], lv), right(zq[:, :], lv), right(d, lv), ALU.mult)\
                        .then_inc(level_ready, 1)

            def cross_decay(hd):
                v.wait_ge(b_ready, hd.H + 1)
                v.wait_ge(level_ready, LEVELS * (hd.H + 1))
                v.tensor_tensor(decay01[:], b[:, P - 1:P], b[:, 2 * P - 1:2 * P], ALU.add)\
                    .then_inc(decay01_ready, 1)

            def cross_products(hd):
                v.wait_ge(cross_exp, hd.H + 1)
                kd, qd = tmp[:, 2, :], tmp[:, 0, :]
                v.tensor_tensor(kd[:, 0:3 * P], kd[:, 0:3 * P], kk[:, 0:3 * P], ALU.mult)
                v.tensor_tensor(row(kd, 3), row(kd, 3), row(kk, 0), ALU.mult)
                v.tensor_tensor(qd[:, 0:2 * P], qd[:, 0:2 * P], zq[:, P:3 * P], ALU.mult)
                q3 = zq[:, 3 * P:4 * P].rearrange("q (o c) -> q o c", o=1).to_broadcast([P, 2, P])
                qd3 = qd[:, 2 * P:4 * P].rearrange("q (o c) -> q o c", o=2)
                v.tensor_tensor(qd3, qd3, q3, ALU.mult).then_inc(cross_ready, 1)

            def counted(value):
                if not isinstance(value, int):
                    v.compute_val(value)
                return value

            def place_levels(hd, levels):
                for lv in levels:
                    bk, at = LEVEL_AT[lv]
                    shape = dict(i=NT, c=1 << lv)
                    scores = counted(LEVELS * hd.H + {0: 2, 2: 3}.get(lv, LEVELS))
                    cross = counted(hd.H + 1)
                    placed = counted(LEVELS * hd.H + lv)
                    v.wait_ge(pool_step, POOL_STEPS)
                    if lv == 0:
                        v.wait_ge(diag_placed, cross)
                    v.wait_ge(level_placed, placed)
                    if lv in (0, 2, 3):
                        v.wait_ge(scores_done, scores)
                    if lv == LEVELS - 1:
                        v.wait_ge(cross_done, cross)
                    v.copy_predicated(diag_blocks(lv), masks[:, lv, :].rearrange("q (i n c) -> q i n c", **shape),
                                      bank[bk][:, at:at + 256].rearrange("q (i n c) -> q i n c", **shape))\
                        .then_inc(level_placed, 1)

            def place_early(hd):
                diag, used = counted(hd.H + 1), counted(hd.H)
                v.wait_ge(pool_step, POOL_STEPS)
                v.wait_ge(diag_done, diag)
                v.wait_ge(o_done, used)
                v.copy_predicated(diag_blocks(), mask_diag[:, :].rearrange("q (i c) -> q i c", i=NT),
                                  bank[2][:, :].rearrange("q (i c) -> q i c", i=NT)).then_inc(diag_placed, 1)
                place_levels(hd, range(EARLY))

            def output_gate(hd):
                for j in range(hd.vt):
                    v.wait_ge(z_evac, hd.unit((4 if hd.gla else 3) + j).u + 1)
                    clamp(hd, "gate", j, zg[:, j, :])
                    apply_silu(hd, "gate", j, zg[:, j, :])

            def head_mean(hd):
                v.wait_ge(norm_ps, hd.H + 1)
                mean_square(norm_bufs, bank[3][:, :], hd.vt * P, norm_step)

            def head_output(hd):
                refine(norm_bufs, norm[:, 1, :], norm_step, 5 * hd.H + 1, norm_act, 2 * hd.H + 2)
                v.wait_ge(norm_step, 5 * hd.H + 5)
                v.wait_ge(sig_step, SIG_V * (hd.sigmoid("gate", hd.vt - 1) + 1))
                for j in range(hd.vt):
                    n = hd.before(1, 3) + 2 * j
                    if j:
                        v.wait_ge(y_step, n)
                    gain = vec2[:, ds(hd.h * 2 + (W_GLA + j), 1)] if hd.gla else vec2[:, ds(hd.h + W_HG, 1)]
                    v.scalar_tensor_tensor(out=norm[:, 2, :], in0=bank[2 + 2 * j][:, :], scalar=gain,
                                           in1=norm[:, 1, :], op0=ALU.mult, op1=ALU.mult).then_inc(y_step, 1)
                    v.wait_ge(y_step, n + 1)
                    done = y_ready if j == hd.vt - 1 else y_step
                    v.tensor_tensor(tile(y, hd.h * 2 + (HG_HEADS + j) if hd.gla else hd.h), norm[:, 2, :],
                                    zg[:, j, :], ALU.mult).then_inc(done, 1)

            def iteration(hd, prev):
                def slot(j):
                    if hd.gla and j == 4:
                        return
                    if hd.gla and j == 5:
                        v.wait_ge(w_lo_ready, hd.unit(5).u + 1)
                    split_lo(hd.unit(j + 1))

                if prev:
                    slot(0)
                    place_levels(prev, range(EARLY, LEVELS))
                    output_gate(prev)
                if prev is None:
                    v.wait_ge(stat_ps, 1)
                    v.tensor_copy(rs_u[:], bank[2][:, :]).then_inc(x_stat_step, 1)
                    v.wait_ge(x_stat_step, 8)
                    for c in range(KT // 4):
                        v.wait_ge(xT_stored[c], 16)
                evacuate(hd.unit(0), conv_in[:, CONV - 1:] if hd.gla else zf[:])
                slot(1)
                if hd.gla:
                    alpha_in(hd)
                    conv(hd, 0, kk[:], hd.h + 4)
                    alpha_out(hd)
                    apply_silu(hd, "conv", 0, kk[:])
                    evacuate(hd.unit(1), conv_in[:, CONV - 1:])
                else:
                    forget_gate(hd)
                    evacuate(hd.unit(1), zq[:])
                slot(2)
                if prev:
                    head_mean(prev)
                if hd.gla:
                    conv(hd, 1, zq[:], hd.h)
                if prev:
                    head_output(prev)
                if hd.gla:
                    apply_silu(hd, "conv", 1, zq[:], float(P) ** -0.5)
                    evacuate(hd.unit(2), conv_in[:, CONV - 1:])
                    slot(3)
                v.wait_ge(sig_step, SIG_V * (hd.operands() + 1))
                if not hd.gla:
                    v.wait_ge(z_evac, hd.unit(1).u + 1)
                if prev is None:
                    v.wait_ge(pool_step, POOL_STEPS)
                level_products(hd, range(EARLY + 1))
                if hd.gla:
                    conv(hd, 2, zv[:, 0, :], hd.h * 2 + 8)
                    apply_silu(hd, "conv", 2, zv[:, 0, :])
                    evacuate(hd.unit(3), conv_in[:, CONV - 1:])
                else:
                    evacuate(hd.unit(2), zv[:, 0, :])
                slot(hd.late - 1)
                if hd.gla:
                    conv(hd, 3, zv[:, 1, :], hd.h * 2 + 9)
                place_early(hd)
                if hd.gla:
                    apply_silu(hd, "conv", 3, zv[:, 1, :])
                level_products(hd, range(EARLY + 1, LEVELS))
                cross_decay(hd)
                if hd.gla:
                    evacuate(hd.unit(4), zg[:, 0, :])
                cross_products(hd)
                if hd.gla:
                    slot(5)
                    evacuate(hd.unit(5), zg[:, 1, :])
                else:
                    evacuate(hd.unit(3), zg[:, 0, :])

            v.wait_ge(vec_ps, 1)
            v.tensor_copy(vec1[:], bank[1][:, 0:P])
            v.tensor_copy(vec2[:], bank[1][:, P:P + N_VEC2]).then_inc(vec_ready, 1)
            logit = vec2[:, W_LB:W_LB + HG_HEADS]
            for k in range(KT):
                v.wait_ge(xT_ps, k + 1)
                v.tensor_copy(h[:, k, :], bank[2 + k % 6][:, :]).then_inc(xT_copied, 1)
                if k >= 1:
                    split_x = k - 1
                    v.wait_ge(u_hi_ready, split_x + 1)
                    v.scalar_tensor_tensor(out=u_lo[:, split_x, :], in0=h[:, split_x, :],
                                           scalar=vec1[:, V_MIX + split_x:V_MIX + split_x + 1],
                                           in1=u_hi[:, split_x, :].bitcast(F32), op0=ALU.mult,
                                           op1=ALU.subtract).then_inc(u_lo_ready, 1)
                if k == 1:
                    v.wait_ge(vec_ready, 1)
                    v.tensor_tensor(lb_e[:], logit, logit, ALU.subtract).then_inc(lb_step, 1)
                if k == 1:
                    split_lo(Unit(0))
                if k == 4:
                    v.wait_ge(lb_exp, 1)
                    v.reciprocal(lb_r[:], lb_e[:]).then_inc(lb_step, 1)
                    v.wait_ge(lb_step, 2)
                    v.tensor_tensor(lb_e[:], lb_e[:], lb_r[:], ALU.mult).then_inc(lb_step, 1)
                    v.wait_ge(lb_step, 3)
                    v.tensor_tensor(lb[:], lb_e[:], lb_e[:], ALU.subtract).then_inc(lb_step, 1)
                    v.wait_ge(lb_step, 4)
                    v.tensor_scalar(minus_one_plus_lb[:], lb[:], -1.0, None, ALU.add).then_inc(lb_step, 1)
            k = KT - 1
            v.wait_ge(u_hi_ready, KT)
            v.scalar_tensor_tensor(out=u_lo[:, k, :], in0=h[:, k, :], scalar=vec1[:, V_MIX + k:V_MIX + k + 1],
                                   in1=u_hi[:, k, :].bitcast(F32), op0=ALU.mult, op1=ALU.subtract)\
                .then_inc(u_lo_ready, 1)
            v.wait_ge(x_squared, NT * NT)
            for n, width in enumerate((2 * NT, NT)):
                v.wait_ge(x_stat_step, n)
                v.tensor_tensor(x_sum[:, 0:width], x_sum[:, 0:width], x_sum[:, width:2 * width], ALU.add)\
                    .then_inc(x_stat_step, 1)
            v.wait_ge(x_stat_step, 2)
            x_rs_bufs = [x_rs[:, i, :] for i in range(3)]
            mean_square(x_rs_bufs, x_sum[:, 0:NT], D, x_stat_step)
            refine(x_rs_bufs, x_rs_bufs[1], x_stat_step, 3, x_stat_act, 2)
            v.wait_ge(x_stat_step, 7)
            v.wait_ge(pool_step, 2)
            for t in range(NT):
                v.tensor_scalar(row(x_rs_diag, t), ident[:], x_rs[:, 1, t:t + 1], None, ALU.mult)\
                    .then_inc(diag_ready, 1)

            iteration(Head("hg", 0), None)
            with v.Fori(1, HG_HEADS) as i:
                iteration(Head("hg", i), Head("hg", i - 1))
            split_lo(Unit(U_CODE + 1))
            evacuate(Unit(U_CODE), code)
            iteration(Head("gla", 0), Head("hg", HG_HEADS - 1))
            with v.Fori(1, GLA_HEADS) as i:
                iteration(Head("gla", i), Head("gla", i - 1))

            last = Head("gla", GLA_HEADS - 1)
            place_levels(last, range(EARLY, LEVELS))

            def split_y(tiles):
                for k in tiles:
                    v.wait_ge(u_hi_ready, KT + k + 1)
                    v.tensor_tensor(u_lo[:, k, :], y[:, k, :], u_hi[:, k, :].bitcast(F32), ALU.subtract)\
                        .then_inc(y_lo_ready, 1)

            output_gate(last)
            split_y(range(POOL_Y, KT - 2))
            split_lo(Unit(U_OUT + 1))
            head_mean(last)
            head_output(last)
            split_y(range(KT - 2, KT))

            def add_to_h(r, bk, m):
                v.wait_ge(z_done, r + 1)
                v.tensor_tensor(tile(h, m), tile(h, m), bank[bk][:, :], ALU.add).then_inc(z_evac, 1)

            v.wait_ge(h_landed[0], 16)
            add_to_h(R_OUT, R_OUT % 2, 0)
            split_lo(Unit(U_OUT + 2))
            add_to_h(R_OUT + 1, (R_OUT + 1) % 2, 1)
            for c in range(1, KT // 4):
                v.wait_ge(h_landed[c], 16)
            with v.Fori(1, KT // 2 - 1) as i:
                for j in range(2):
                    unit = Unit(U_OUT + j, 2, i)
                    split_lo(unit.next())
                    add_to_h(unit.u, unit.slot, 2 * i + j)
            split_lo(Unit(U_MLP - 1))
            add_to_h(R_MLP - 2, (R_MLP - 2) % 2, KT - 2)
            split_lo(Unit(U_MLP))

            def split_h(k, at, n):
                v.wait_ge(u_hi_ready, KT * n + k + 1)
                v.scalar_tensor_tensor(out=u_lo[:, k, :], in0=h[:, k, :], scalar=vec1[:, at + k:at + k + 1],
                                       in1=u_hi[:, k, :].bitcast(F32), op0=ALU.mult, op1=ALU.subtract)\
                    .then_inc(u_lo_ready, 1)

            for k in range(KT):
                if k == KT - 1:
                    add_to_h(R_MLP - 1, (R_MLP - 1) % 2, k)
                split_h(k, V_MLP, 2)
            for f in range(2):
                v.wait_ge(p_hi_ready, f + 1)
                v.tensor_tensor(p_lo[:, f, :], bank[3 + f][:, :], p_hi[:, f, :].bitcast(F32), ALU.subtract)\
                    .then_inc(p_lo_ready, 1)

            def a_low(c, j):
                v.wait_ge(a_hi_ready, CH * c + j + 1)
                v.tensor_tensor(a_lo[:, j, :], work[:, j % 2, :], a_hi[:, j, :].bitcast(F32), ALU.subtract)\
                    .then_inc(a_lo_ready, 1)

            def mlp_chunk(c, first=False, final=False):
                for j in range(CH):
                    unit = Unit(U_MLP + j, MLP_UNITS, c)
                    split_lo(unit.next())
                    if first and j == 0:
                        stream_mean(1, norm2_bufs)
                        stream_refine(1, norm2_bufs)
                        v.wait_ge(stat_step, 5)
                    if j >= 1:
                        a_low(c, j - 1)
                    v.wait_ge(z_done, R_MLP + j + MLP_RESULTS * c + 1)
                    if j >= 2:
                        v.wait_ge(a_hi_ready, CH * c + j - 1)
                    v.scalar_tensor_tensor(out=relu[:, j % 2, :], in0=bank[unit.slot][:, :], scalar=0.0,
                                           in1=rs_u[:], op0=ALU.max, op1=ALU.mult).then_inc(z_evac, 1)
                for j in range(CH):
                    unit = Unit(U_MLP + CH + j, MLP_UNITS, c)
                    if j == 0:
                        a_low(c, CH - 1)
                    split_lo(unit.next())
                    if final and j:
                        split_h(2 * j - 2, V_PLE, 3)
                        split_h(2 * j - 1, V_PLE, 3)
                    for m in range(2):
                        r = R_MLP + CH + 2 * j + m
                        add_to_h(r + MLP_RESULTS * c, r % 2, 2 * j + m)

            mlp_chunk(0, first=True)
            with v.Fori(1, CHUNKS - 1) as c:
                mlp_chunk(c)
            mlp_chunk(CHUNKS - 1, final=True)

            for m in range(KT):
                v.wait_ge(z_done, R_PP + m + 1)
                v.tensor_copy(pp[:, m, :], bank[(R_PP + m) % 2][:, :]).then_inc(z_evac, 1)
                if m < 2:
                    split_h(KT - 2 + m, V_PLE, 3)
                if m == 2:
                    split_lo(Unit(U_PP + 1))
                if m == 9:
                    split_lo(Unit(U_PP + 2))
            stream_mean(2, norm2_bufs)
            stream_refine(2, norm2_bufs)
            v.wait_ge(stat_step, 10)

            def gate_slot(unit, m, split):
                if split:
                    split_lo(unit.next())
                n = 5 * m
                e, inv = work[:, 0, :], relu[:, 0, :]
                v.wait_ge(z_done, R_PG + m + 1)
                v.tensor_tensor(e, bank[(R_PG + unit.first - U_PG) % 2][:, :], rs_u[:], ALU.mult).then_inc(z_evac, 1)
                v.wait_ge(z_evac, R_PG + 1 + m)
                v.tensor_scalar(e, e, -EXP_MAX, None, ALU.max).then_inc(pg_step, 1)
                v.wait_ge(pg_act, 3 * m + 3)
                v.scalar_tensor_tensor(out=e, in0=e, scalar=1.0, in1=inv, op0=ALU.add, op1=ALU.mult)\
                    .then_inc(pg_step, 1)
                v.wait_ge(pg_step, n + 2)
                v.scalar_tensor_tensor(out=e, in0=e, scalar=2.0, in1=inv, op0=ALU.subtract, op1=ALU.mult)\
                    .then_inc(pg_step, 1)
                v.wait_ge(pg_step, n + 3)
                v.scalar_tensor_tensor(out=e, in0=e, scalar=-1.0, in1=tile(pp, m), op0=ALU.mult, op1=ALU.mult)\
                    .then_inc(pg_step, 1)
                v.wait_ge(pg_step, n + 4)
                v.tensor_tensor(tile(h, m), tile(h, m), e, ALU.add).then_inc(pg_step, 1)
                v.wait_ge(pg_step, n + 5)
                v.wait_ge(turned, m + 1)
                v.tensor_scalar(work[:, 1, :], tile(h, m), vec1[:, ds(m + V_FINAL, 1)], None, ALU.mult)\
                    .then_inc(hg_ready, 1)

            with v.Fori(0, KT // 2 - 1) as i:
                for j in range(2):
                    gate_slot(Unit(U_PG + j, 2, i), 2 * i + j, True)
            gate_slot(Unit(UNITS - 2), KT - 2, True)
            gate_slot(Unit(UNITS - 1), KT - 1, False)

            v.wait_ge(stat_ps, 4)
            tok_bufs = [tok[:, i, :] for i in range(3)]
            mean_square(tok_bufs, bank[2][:, 0:NT], D, tok_step)
            refine(tok_bufs, tok[:, 1, :], tok_step, 1, tok_act, 2)
            v.wait_ge(tok_step, 5)
            v.wait_ge(outT_placed, KT)
            for t in range(NT - 1):
                part = h[:, :, t * P:(t + 1) * P]
                v.tensor_scalar(part, part, tok[:, 1, t:t + 1], None, ALU.mult).then_inc(tok_scaled, 1)

        @block.tensor
        def _(pe):
            def tri(ps, whi, wlo, xhi, xlo, start, stop):
                pe.matmul(ps, whi, xhi, start=start, stop=False)
                pe.matmul(ps, whi, xlo, start=False, stop=False)
                return pe.matmul(ps, wlo, xhi, start=False, stop=stop)

            def wtiles(unit, k, m=0, cols=P):
                at = k * cols + m * P
                return w_hi[:, unit.slot, at:at + P], w_lo[:, unit.slot, at:at + P]

            def product(unit, r, bk, between=(), rows=range(KT), read=None):
                pe.wait_ge(w_lo_ready, unit.u + 1)
                if not isinstance(r, int) or r >= 2:
                    pe.wait_ge(z_evac, r - 1)
                for k in rows:
                    if k in between:
                        between[k]()
                    last = tri(bank[bk][:, :], *wtiles(unit, k), u_hi[:, k, :], u_lo[:, k, :], k == 0, k == KT - 1)
                    if read is not None and k < KT - 1:
                        last.then_inc(read, 1)
                if rows[-1] == KT - 1:
                    last.then_inc(z_done, 1)

            def early_scores(hd):
                pe.wait_ge(sig_step, SIG_V * (hd.operands() + 1))
                if not hd.gla:
                    pe.wait_ge(z_evac, hd.unit(1).u + 1)
                pe.wait_ge(y_ready, hd.H)
                for t in range(NT):
                    last = pe.matmul(bank[2][:, t * P:(t + 1) * P], row(kk, t), row(zq, t), start=True, stop=True)
                last.then_inc(diag_done, 1)
                for lv in range(EARLY):
                    level_scores(hd, lv)

            def level_scores(hd, lv):
                pe.wait_ge(level_ready, LEVELS * hd.H + lv + 1)
                bk, at = LEVEL_AT[lv]
                for t in range(NT):
                    last = pe.matmul(bank[bk][:, at + t * 64:at + (t + 1) * 64], kl[:, lv % 4, t * P:(t + 1) * P],
                                     ql[:, lv % 4, t * 64:(t + 1) * 64], start=True, stop=True)
                last.then_inc(scores_done, 1)

            def late_scores(hd):
                pe.wait_ge(level_placed, LEVELS * hd.H + EARLY)
                for lv in range(EARLY, LEVELS):
                    level_scores(hd, lv)
                pe.wait_ge(cross_ready, hd.H + 1)
                pe.wait_ge(cross_placed, hd.H)
                kd, qd = tmp[:, 2, :], tmp[:, 0, :]
                pe.matmul(bank[6][:, 2 * P:3 * P], row(kd, 0), row(qd, 0), start=True, stop=True)
                pe.matmul(bank[6][:, 3 * P:4 * P], row(kd, 2), row(qd, 3), start=True, stop=True)
                pe.matmul(bank[7][:, 0:2 * P], row(kd, 3), qd[:, P:3 * P], start=True, stop=True)
                pe.matmul(bank[7][:, 2 * P:4 * P], row(kd, 1), qd[:, P:3 * P], start=True, stop=True)\
                    .then_inc(cross_done, 1)

            def values(hd):
                if hd.gla:
                    pe.wait_ge(sig_step, SIG_V * (hd.sigmoid("conv", 3) + 1))
                else:
                    pe.wait_ge(z_evac, hd.unit(2).u + 1)
                for v in range(hd.vt):
                    for t in range(NT):
                        last = pe.transpose(bank[2 + v][:, t * P:(t + 1) * P], zv[:, v, t * P:(t + 1) * P], ident[:, :])
                last.then_inc(vT_done, 1)

            def outputs(hd):
                pe.wait_ge(level_placed, LEVELS * (hd.H + 1))
                pe.wait_ge(cross_placed, hd.H + 1)
                pe.wait_ge(v_placed, hd.H + 1)
                for v in range(hd.vt):
                    for t in range(NT):
                        last = pe.matmul(bank[2 + 2 * v][:, t * P:S], V[:, t, v * P:(v + 1) * P],
                                         A[:, t * S:3 * P * t + S], start=(t == 0), stop=(t == NT - 1))
                last.then_inc(o_done, 1)

            def square_sums(hd):
                if isinstance(hd.h, int) and hd.H == HEADS - 1:
                    pe.wait_ge(osq_act, 2 * GLA_HEADS)
                    pe.matmul(bank[3][:, :], ones[:, :], norm[:, 0, :], start=True, stop=False)
                    pe.matmul(bank[3][:, :], ones[:, :], norm[:, 1, :], start=False, stop=True).then_inc(norm_ps, 1)
                    return
                if hd.gla:
                    pe.wait_ge(osq_ready, hd.h + 1)
                else:
                    pe.wait_ge(osq_ready_hg, hd.h + 1)
                pe.matmul(bank[3][:, :], ones[:, :], norm[:, 0, :], start=True, stop=True).then_inc(norm_ps, 1)

            def alpha(hd):
                pe.wait_ge(alpha_w, hd.h + 1)
                pe.wait_ge(z_evac, U_CODE + 1)
                pe.wait_ge(level_placed, LEVELS * hd.H)
                pe.matmul(bank[5][:, :], w_gate_h[:, :], code, start=True, stop=True).then_inc(alpha_ps, 1)

            def stream_sum(n):
                pe.wait_ge(sum_done, (KT + 1) * n)
                pe.matmul(bank[2][:, :], ones[:, :], sum_sq[:, :], start=True, stop=True).then_inc(stat_ps, 1)

            def iteration(hd, prev, between=()):
                if prev:
                    between = {4: lambda: values(prev)}
                product(hd.unit(0), hd.unit(0).u, hd.unit(0).slot, between)
                if prev is None:
                    pe.wait_ge(diag_ready, NT)
                    pe.matmul(bank[2][:, :], ones[:, :], x_rs_diag, start=True, stop=True).then_inc(stat_ps, 1)
                if prev:
                    outputs(prev)
                if hd.gla:
                    alpha(hd)
                product(hd.unit(1), hd.unit(1).u, hd.unit(1).slot)
                if prev:
                    square_sums(prev)
                for j in range(2, hd.units):
                    product(hd.unit(j), hd.unit(j).u, hd.unit(j).slot, read=u_read if j == GLA_UNITS - 1 else None)
                    if j == hd.late - 2:
                        early_scores(hd)
                late_scores(hd)

            pe.wait_ge(rows_landed, 16 * 9)
            pe.wait_ge(pool_step, 2)
            pe.transpose(bank[1][:, 0:P], rows1, ident[:, :])
            pe.transpose(bank[1][:, P:P + N_VEC2], rows2[0:N_VEC2, :], ident[0:N_VEC2, 0:N_VEC2]).then_inc(vec_ps, 1)

            def x_tile(k):
                pe.wait_ge(x_landed[k // 4], 16)
                if k >= 6:
                    pe.wait_ge(xT_copied, k - 5)
                for t in range(NT):
                    last = pe.transpose(bank[2 + k % 6][:, t * P:(t + 1) * P], x_in[:, t, k * P:(k + 1) * P],
                                        ident[:, :])
                last.then_inc(xT_ps, 1)

            def ahead_of(k):
                def run():
                    if k + 4 < KT:
                        x_tile(k + 4)
                    pe.wait_ge(u_lo_ready, k + 1)
                return run

            for k in range(4):
                x_tile(k)
            pe.wait_ge(pool_step, 3)
            iteration(Head("hg", 0), None, {k: ahead_of(k) for k in range(KT)})
            with pe.Fori(1, HG_HEADS) as i:
                iteration(Head("hg", i), Head("hg", i - 1))
            product(Unit(U_CODE), U_CODE, U_CODE % 2)
            iteration(Head("gla", 0), Head("hg", HG_HEADS - 1))
            with pe.Fori(1, GLA_HEADS) as i:
                iteration(Head("gla", i), Head("gla", i - 1))

            last = Head("gla", GLA_HEADS - 1)

            def y_tile(k):
                def run():
                    if k == 1:
                        values(last)
                    if k == 4:
                        outputs(last)
                    if k == 12:
                        square_sums(last)
                    if k < POOL_Y:
                        pe.wait_ge(u_lo_ready, KT + k + 1)
                    else:
                        pe.wait_ge(y_lo_ready, k - POOL_Y + 1)
                return run

            others, own = range(KT - 2), range(KT - 2, KT)
            first, second = (Unit(U_OUT), U_OUT, U_OUT % 2), (Unit(U_OUT + 1), U_OUT + 1, (U_OUT + 1) % 2)
            product(*first, {k: y_tile(k) for k in others}, others)
            product(*second, (), others)
            product(*first, {k: y_tile(k) for k in own}, own)
            product(*second, (), own)
            with pe.Fori(1, KT // 2) as i:
                for j in range(2):
                    unit = Unit(U_OUT + j, 2, i)
                    product(unit, unit.u, unit.slot, read=u_read if j else None)

            pe.wait_ge(p_landed, 16)
            for f in range(2):
                for t in range(NT):
                    last_t = pe.transpose(bank[3 + f][:, t * P:(t + 1) * P], p_in[:, t, f * P:(f + 1) * P], ident[:, :])
            last_t.then_inc(turned, 1)

            def mlp_chunk(c, first=False):
                for j in range(CH):
                    unit = Unit(U_MLP + j, MLP_UNITS, c)
                    r = R_MLP + j

                    def h_tile(k):
                        def run():
                            if k == 10:
                                stream_sum(1)
                            pe.wait_ge(u_lo_ready, KT + POOL_Y + k + 1)
                        return run

                    product(unit, r + MLP_RESULTS * c, r % 2, {k: h_tile(k) for k in range(KT)} if first and j == 0 else ())
                for j in range(CH):
                    unit = Unit(U_MLP + CH + j, MLP_UNITS, c)
                    pe.wait_ge(w_lo_ready, unit.u + 1)
                    for m in range(2):
                        r = R_MLP + CH + 2 * j + m
                        pe.wait_ge(z_evac, r + MLP_RESULTS * c - 1)
                        for k in range(CH):
                            if j == 0 and m == 0:
                                pe.wait_ge(a_lo_ready, CH * c + k + 1)
                            last_t = tri(bank[r % 2][:, :], *wtiles(unit, k, m, 2 * P), a_hi[:, k, :], a_lo[:, k, :],
                                         k == 0, k == CH - 1)
                        last_t.then_inc(z_done, 1)

            mlp_chunk(0, True)
            with pe.Fori(1, CHUNKS) as c:
                mlp_chunk(c)

            pe.wait_ge(p_lo_ready, 2)
            for m in range(KT):
                unit = Unit(U_PP + m // 8)
                if m % 8 == 0:
                    pe.wait_ge(w_lo_ready, unit.u + 1)
                pe.wait_ge(z_evac, R_PP + m - 1)
                for k in range(2):
                    last_t = tri(bank[(R_PP + m) % 2][:, :], *wtiles(unit, k, m % 8, D // 2), p_hi[:, k, :],
                                 p_lo[:, k, :], k == 0, k == 1)
                last_t.then_inc(z_done, 1)
                if m == 3:
                    stream_sum(2)
            pe.wait_ge(u_lo_ready, 3 * KT + POOL_Y)

            def output_tile(slot, m_plus_1):
                pe.wait_ge(hg_ready, m_plus_1)
                if not isinstance(m_plus_1, int) or m_plus_1 > 2:
                    pe.wait_ge(outT_placed, m_plus_1 - 2)
                for t in range(NT):
                    last_t = pe.transpose(bank[3 + slot][:, t * P:(t + 1) * P], work[:, 1, t * P:(t + 1) * P],
                                          ident[:, :])
                last_t.then_inc(turned, 1)

            product(Unit(U_PG), R_PG, R_PG % 2)
            product(Unit(U_PG + 1), R_PG + 1, (R_PG + 1) % 2)
            output_tile(U_PG % 2, 1)
            with pe.Fori(1, KT // 2) as i:
                for j in range(2):
                    unit = Unit(U_PG + j, 2, i)
                    r = R_PG + j
                    product(unit, r + 2 * i, r % 2)
                    output_tile(1 - unit.slot, 2 * i + j)
            output_tile((UNITS - 1) % 2, KT)
            pe.wait_ge(sum_done, (KT + 1) * 3 - 1)
            pe.wait_ge(last_squared, 1)
            for t in range(NT):
                pe.matmul(bank[2][:, t:t + 1], sum_sq[:, t * P:(t + 1) * P], ones[:, 0:1], start=True, stop=False)
                last_t = pe.matmul(bank[2][:, t:t + 1], relu[:, 1, t * P:(t + 1) * P], ones[:, 0:1],
                                   start=False, stop=True)
            last_t.then_inc(stat_ps, 1)


_INS = ["x", "p", "g_mix", "w_in", "lb_logits", "g_hg_norm", "conv_w", "w_gla_gate", "b_gla_gate", "g_gla_norm",
        "w_out", "g_mlp", "w_up", "w_down", "g_ple", "w_pg", "w_pp", "g_final"]


def kernel(**inputs):
    import numpy as np
    import concourse.bacc as bacc
    from concourse.bass_utils import run_bass_kernel_spmd

    nc = bacc.Bacc("TRN2", target_bir_lowering=False, num_devices=1)
    arrays, args = {}, []
    for name in _INS:
        a = np.ascontiguousarray(inputs[name])
        arrays[f"in_{name}"] = a
        args.append(nc.dram_tensor(f"in_{name}", a.shape, mybir.dt.from_np(a.dtype), kind="ExternalInput").ap())
    args.append(nc.dram_tensor("out_0", (1, S, D), F32, kind="ExternalOutput").ap())
    build(nc, *args)
    r = run_bass_kernel_spmd(nc, [arrays], core_ids=[0])
    return r.results[0]["out_0"]
```
